# Optimizing a Trainium2 kernel written in Bass

```python
import math
import jax, jax.numpy as jnp
from jax import lax
import numpy as np

D_MODEL = 1024
BATCH = 1
SEQ = 256
DEPTH = 1

D_MIX = D_MODEL
SSM_WIDTH = D_MIX // 2
POOL_WIDTH = D_MIX // 4
CONV_WIDTH = D_MIX - SSM_WIDTH - POOL_WIDTH
SSM_GROUP = 16
SSM_GROUPS = SSM_WIDTH // SSM_GROUP
SSM_STATE = 64
STEP_MIN = 1e-3
STEP_MAX = 1e-1
LAMBDA_RE_MAX = -1e-4
POOL_WINDOWS = (2, 4, 8, 16)
POOL_GROUP = POOL_WIDTH // len(POOL_WINDOWS)
CONV_K = 3
IN_WIDTH = SSM_WIDTH + POOL_WIDTH + 3 * CONV_WIDTH
N_EXPERTS = 32
TOP_K = 4
D_EXPERT = D_MODEL
SWIGLU_LIMIT = 7.0
SWIGLU_ALPHA = 1.702
EXPERT_BLOCK = 256
NORM_EPS = 1e-5

kernel_name = 'hymba_s5_pool_shortconv_moe'

def rmsnorm(x, g):
    xf = x.astype(jnp.float32)
    r = lax.rsqrt(jnp.mean(xf * xf, axis=-1, keepdims=True) + NORM_EPS)
    return (xf * r).astype(x.dtype) * g

def _complex_linear_combine(e1, e2):
    a1r, a1i, b1r, b1i = e1
    a2r, a2i, b2r, b2i = e2
    ar = a2r * a1r - a2i * a1i
    ai = a2r * a1i + a2i * a1r
    br = a2r * b1r - a2i * b1i + b2r
    bi = a2r * b1i + a2i * b1r + b2i
    return (ar, ai, br, bi)

def s5_mixer(u, lam_re, lam_im, b_re, b_im, c_re, c_im, d_skip, log_step, w_glu, b_glu):
    f32 = jnp.float32
    bsz, L, _ = u.shape
    uf = u.astype(f32)
    ug = uf.reshape(bsz, L, SSM_GROUPS, SSM_GROUP)
    lr = jnp.minimum(lam_re.astype(f32), LAMBDA_RE_MAX)
    li = lam_im.astype(f32)
    step = jnp.exp(log_step.astype(f32))[:, None]
    mag = jnp.exp(lr * step)
    ar = mag * jnp.cos(li * step)
    ai = mag * jnp.sin(li * step)
    nr = ar - 1.0
    den = lr * lr + li * li
    kr = (nr * lr + ai * li) / den
    ki = (ai * lr - nr * li) / den
    bre = b_re.astype(f32)
    bim = b_im.astype(f32)
    bbar_r = kr[..., None] * bre - ki[..., None] * bim
    bbar_i = kr[..., None] * bim + ki[..., None] * bre
    bu_r = jnp.einsum('blgh,gph->blgp', ug, bbar_r)
    bu_i = jnp.einsum('blgh,gph->blgp', ug, bbar_i)
    a_r = jnp.broadcast_to(ar[None, None], (1, L, SSM_GROUPS, SSM_STATE))
    a_i = jnp.broadcast_to(ai[None, None], (1, L, SSM_GROUPS, SSM_STATE))
    _, _, h_r, h_i = lax.associative_scan(_complex_linear_combine, (a_r, a_i, bu_r, bu_i), axis=1)
    y = (jnp.einsum('blgp,ghp->blgh', h_r, c_re.astype(f32))
         - jnp.einsum('blgp,ghp->blgh', h_i, c_im.astype(f32)))
    y = y.reshape(bsz, L, SSM_WIDTH) + d_skip.astype(f32) * uf
    z = jax.nn.gelu(y)
    out = z * jax.nn.sigmoid(z @ w_glu.astype(f32) + b_glu.astype(f32))
    return out.astype(u.dtype)

def causal_window_mean(z, w):
    L = z.shape[1]
    cs = jnp.cumsum(z, axis=1)
    cs_pad = jnp.pad(cs, ((0, 0), (w, 0), (0, 0)))
    total = cs_pad[:, w:] - cs_pad[:, :L]
    count = jnp.minimum(jnp.arange(1, L + 1), w).astype(jnp.float32)
    return total / count[None, :, None]

def pool_mixer(p, pool_w, pool_scale):
    f32 = jnp.float32
    bsz, L, _ = p.shape
    pf = p.astype(f32).reshape(bsz, L, len(POOL_WINDOWS), POOL_GROUP)
    pooled = jnp.stack([causal_window_mean(pf[:, :, i], w) - pf[:, :, i]
                        for i, w in enumerate(POOL_WINDOWS)], axis=2)
    mixed = jnp.einsum('blgc,gcd->blgd', pooled, pool_w.astype(f32)).reshape(bsz, L, POOL_WIDTH)
    return (mixed * pool_scale.astype(f32)).astype(p.dtype)

def short_conv_mixer(bg, cg, hv, conv_w):
    L = hv.shape[1]
    z = cg * hv
    zp = jnp.pad(z, ((0, 0), (CONV_K - 1, 0), (0, 0)))
    y = conv_w[0] * zp[:, 0:L]
    for k in range(1, CONV_K):
        y = y + conv_w[k] * zp[:, k:k + L]
    return bg * y

def moe_ffn(h, router_w, router_b, w_gu, b_gu, w_dn, b_dn):
    bsz, L, D = h.shape
    N = bsz * L
    NK = N * TOP_K
    x = h.reshape(N, D)
    logits = (x @ router_w + router_b).astype(jnp.float32)
    top_vals, top_idx = lax.top_k(logits, TOP_K)
    gates = jax.nn.softmax(top_vals, axis=-1)
    flat_e = top_idx.reshape(NK).astype(jnp.int32)
    flat_tok = jnp.arange(NK, dtype=jnp.int32) // TOP_K
    flat_gate = gates.reshape(NK)
    order = jnp.argsort(flat_e)
    sorted_e = flat_e[order]
    counts = jnp.bincount(flat_e, length=N_EXPERTS).astype(jnp.int32)
    padded = (counts + EXPERT_BLOCK - 1) // EXPERT_BLOCK * EXPERT_BLOCK
    padded_end = jnp.cumsum(padded)
    padded_start = padded_end - padded
    start = jnp.cumsum(counts) - counts
    dest = padded_start[sorted_e] + jnp.arange(NK, dtype=jnp.int32) - start[sorted_e]
    n_blocks = -(-(NK + N_EXPERTS * (EXPERT_BLOCK - 1)) // EXPERT_BLOCK)
    R = n_blocks * EXPERT_BLOCK
    row_tok = jnp.full((R,), N, jnp.int32).at[dest].set(flat_tok[order])
    row_gate = jnp.zeros((R,), jnp.float32).at[dest].set(flat_gate[order])
    block_start = jnp.arange(n_blocks, dtype=jnp.int32) * EXPERT_BLOCK
    block_e = jnp.minimum(jnp.searchsorted(padded_end, block_start, side='right'), N_EXPERTS - 1)
    x_pad = jnp.concatenate([x, jnp.zeros((1, D), x.dtype)], axis=0)
    xs = x_pad[row_tok].reshape(n_blocks, EXPERT_BLOCK, D)

    def expert_block(args):
        xb, e = args
        gu = xb @ w_gu[e] + b_gu[e]
        gate = jnp.minimum(gu[:, :D_EXPERT], SWIGLU_LIMIT)
        up = jnp.clip(gu[:, D_EXPERT:], -SWIGLU_LIMIT, SWIGLU_LIMIT)
        act = gate * jax.nn.sigmoid(SWIGLU_ALPHA * gate) * (up + 1.0)
        return act @ w_dn[e] + b_dn[e]

    ys = lax.map(expert_block, (xs, block_e)).reshape(R, D)
    ys = ys * row_gate[:, None].astype(ys.dtype)
    out = jax.ops.segment_sum(ys, row_tok, num_segments=N + 1)[:N]
    return out.reshape(bsz, L, D)

def setup_inputs(seed: int = 0) -> dict:
    key = jax.random.key(seed)
    ks = jax.random.split(key, 28)
    f32 = jnp.float32

    def nrm(k, shape, scale):
        return scale * jax.random.normal(k, shape, f32)

    G, P, H = SSM_GROUPS, SSM_STATE, SSM_GROUP
    return {
        'x': nrm(ks[0], (BATCH, SEQ, D_MODEL), 1.0),
        'norm_mix': 1.0 + nrm(ks[1], (DEPTH, D_MODEL), 0.02),
        'w_in': nrm(ks[2], (DEPTH, D_MODEL, IN_WIDTH), D_MODEL ** -0.5),
        'ssm_lam_re': -0.5 + nrm(ks[3], (DEPTH, G, P), 0.01),
        'ssm_lam_im': math.pi * jnp.arange(P, dtype=f32) + nrm(ks[4], (DEPTH, G, P), 0.01),
        'ssm_b_re': nrm(ks[5], (DEPTH, G, P, H), (2 * H) ** -0.5),
        'ssm_b_im': nrm(ks[6], (DEPTH, G, P, H), (2 * H) ** -0.5),
        'ssm_c_re': nrm(ks[7], (DEPTH, G, H, P), (2 * P) ** -0.5),
        'ssm_c_im': nrm(ks[8], (DEPTH, G, H, P), (2 * P) ** -0.5),
        'ssm_d': nrm(ks[9], (DEPTH, SSM_WIDTH), 1.0),
        'ssm_log_step': jax.random.uniform(ks[10], (DEPTH, G), f32, math.log(STEP_MIN), math.log(STEP_MAX)),
        'ssm_w_glu': nrm(ks[11], (DEPTH, SSM_WIDTH, SSM_WIDTH), SSM_WIDTH ** -0.5),
        'ssm_b_glu': nrm(ks[12], (DEPTH, SSM_WIDTH), 0.02),
        'pool_w': nrm(ks[13], (DEPTH, len(POOL_WINDOWS), POOL_GROUP, POOL_GROUP), POOL_GROUP ** -0.5),
        'pool_scale': 1.0 + nrm(ks[14], (DEPTH, POOL_WIDTH), 0.1),
        'conv_w': nrm(ks[15], (DEPTH, CONV_K, CONV_WIDTH), CONV_K ** -0.5),
        'branch_norm': 1.0 + nrm(ks[16], (DEPTH, D_MIX), 0.02),
        'w_out': nrm(ks[17], (DEPTH, D_MIX, D_MODEL), D_MIX ** -0.5),
        'norm_ffn': 1.0 + nrm(ks[18], (DEPTH, D_MODEL), 0.02),
        'router_w': nrm(ks[19], (DEPTH, D_MODEL, N_EXPERTS), D_MODEL ** -0.5),
        'router_b': nrm(ks[20], (DEPTH, N_EXPERTS), 0.01),
        'w_gate_up': nrm(ks[21], (DEPTH, N_EXPERTS, D_MODEL, 2 * D_EXPERT), D_MODEL ** -0.5),
        'b_gate_up': nrm(ks[22], (DEPTH, N_EXPERTS, 2 * D_EXPERT), 0.02),
        'w_down': nrm(ks[23], (DEPTH, N_EXPERTS, D_EXPERT, D_MODEL), D_EXPERT ** -0.5),
        'b_down': nrm(ks[24], (DEPTH, N_EXPERTS, D_MODEL), 0.02),
        'final_norm': 1.0 + nrm(ks[25], (D_MODEL,), 0.02),
    }

def reference(x, norm_mix, w_in, ssm_lam_re, ssm_lam_im, ssm_b_re, ssm_b_im, ssm_c_re, ssm_c_im,
              ssm_d, ssm_log_step, ssm_w_glu, ssm_b_glu, pool_w, pool_scale, conv_w, branch_norm,
              w_out, norm_ffn, router_w, router_b, w_gate_up, b_gate_up, w_down, b_down, final_norm):
    s0 = SSM_WIDTH
    s1 = s0 + POOL_WIDTH
    splits = [s0, s1, s1 + CONV_WIDTH, s1 + 2 * CONV_WIDTH]
    for l in range(DEPTH):
        hn = rmsnorm(x, norm_mix[l])
        proj = hn @ w_in[l]
        u, p, bg, cg, hv = jnp.split(proj, splits, axis=-1)
        y_ssm = s5_mixer(u, ssm_lam_re[l], ssm_lam_im[l], ssm_b_re[l], ssm_b_im[l],
                         ssm_c_re[l], ssm_c_im[l], ssm_d[l], ssm_log_step[l],
                         ssm_w_glu[l], ssm_b_glu[l])
        y_pool = pool_mixer(p, pool_w[l], pool_scale[l])
        y_conv = short_conv_mixer(bg, cg, hv, conv_w[l])
        g = branch_norm[l]
        mixed = jnp.concatenate([rmsnorm(y_ssm, g[:s0]),
                                 rmsnorm(y_pool, g[s0:s1]),
                                 rmsnorm(y_conv, g[s1:])], axis=-1)
        x = x + mixed @ w_out[l]
        x = x + moe_ffn(rmsnorm(x, norm_ffn[l]), router_w[l], router_b[l],
                        w_gate_up[l], b_gate_up[l], w_down[l], b_down[l])
    return rmsnorm(x, final_norm)


_drawn_inputs = setup_inputs


def setup_inputs(seed=0):
    import zlib

    import numpy as np

    out = dict(_drawn_inputs(seed))
    spreads = {}
    factors = {'ssm_lam_re': 8.0,
     'ssm_b_glu': 5.025,
     'router_b': 3.367,
     'b_gate_up': 6.834,
     'b_down': 7.831,
     'final_norm': 2.804}
    for name, (base, spread) in spreads.items():
        noise = np.random.default_rng([zlib.crc32(name.encode()), seed]).standard_normal(out[name].shape)
        drawn = base * np.exp(spread * noise) if base else spread * noise
        out[name] = __import__('jax').numpy.asarray(drawn.astype(out[name].dtype))
    for name, factor in factors.items():
        out[name] = (out[name] * factor).astype(out[name].dtype)
    return out
```

```python
import math
from contextlib import ExitStack

import numpy as np

import concourse.bass as bass
from concourse import mybir

F32 = mybir.dt.float32
I32 = mybir.dt.int32
ALU = mybir.AluOpType
ACT = mybir.ActivationFunctionType
AX_X = mybir.AxisListType.X

P = 128
TOK = 256
D = 1024
NT = TOK // P
NK = D // P
G, ST, H = 32, 64, 16
L8 = 8
NC = TOK // L8
NP = G // 2
NE = 32
TOPK = 4
FE = 1024
SLOTS = 64
ROUNDS = TOK // SLOTS
PAIRS = NE // 2
PADT = 16
WINDOWS = (2, 4, 8, 16)
EPS = 1e-5
LIMIT, ALPHA = 7.0, 1.702
LAMBDA_RE_MAX = -1e-4

RING = 16
OWN_SLOTS = 12
UNIT = 2048
FRONT_UNITS = 11
PAIR_UNITS = 24

C_ID, C_ONE, C_SU, C_D32, C_D16, C_IOTA, C_RC, C_END = 0, 128, 256, 384, 416, 432, 496, 1008
V_NM, V_BN, V_BG, V_PS, V_CW, V_NF, V_DS, V_RB, V_PW, V_RW, V_END = 0, 8, 16, 20, 22, 28, 36, 40, 72, 328, 584
S_LR, S_LI, S_LS, S_BR, S_BI, S_CR, S_CI, S_KR, S_KI, S_END = 0, 16, 32, 48, 304, 560, 816, 1072, 1584, 2096

BY_HALF = (0, 2, 1, 3)

LN2_HI, LN2_LO = 0.693145751953125, 1.428606765330187e-06
MAGIC = 1.5 * 2.0 ** 23
TWO_PI_A, TWO_PI_B = 6.28125, 2029.0 / 2 ** 20
TWO_PI_C = 2 * math.pi - TWO_PI_A - TWO_PI_B
GELU_C, GELU_K = 0.044715, math.sqrt(2.0 / math.pi)


class Signals:

    def __init__(self, sem):
        self.ld_ssm = sem("ld_ssm")
        self.ld_cs = sem("ld_cs")
        self.ld_vec = sem("ld_vec")
        self.ld_xt = [sem("ld_xt0"), sem("ld_xt1")]
        self.ld_cst = sem("ld_cst")
        self.ld_col = sem("ld_col")
        self.ld_x = sem("ld_x")
        self.ld_bias = sem("ld_bias")
        self.ld_bdn = sem("ld_bdn")
        self.bdn_ready = sem("bdn_ready")
        self.ld_fn = sem("ld_fn")
        self.unit_used = sem("unit_used")
        self.sq_x = sem("sq_x")
        self.sq_sum = sem("sq_sum")
        self.ss_x = sem("ss_x")
        self.sd_x = sem("sd_x")
        self.rbx_ready = sem("rbx_ready")
        self.xg_ready = sem("xg_ready")
        self.rcq_ready = sem("rcq_ready")
        self.angle = sem("angle")
        self.trig = sem("trig")
        self.pow_ready = sem("pow_ready")
        self.gb_ready = sem("gb_ready")
        self.hc_ready = sem("hc_ready")
        self.proj_full = sem("proj_full")
        self.proj_out = sem("proj_out")
        self.z_ready = sem("z_ready")
        self.ut_full = sem("ut_full")
        self.u_ready = sem("u_ready")
        self.gbt_full = sem("gbt_full")
        self.gbt_dve = sem("gbt_dve")
        self.gbt_act = sem("gbt_act")
        self.k_full = sem("k_full")
        self.k_out = sem("k_out")
        self.k_skip = sem("k_skip")
        self.kt_full = sem("kt_full")
        self.kt_out = sem("kt_out")
        self.toep_zero = sem("toep_zero")
        self.toep_moved = sem("toep_moved")
        self.vt_full = sem("vt_full")
        self.vt_out = sem("vt_out")
        self.v_full = sem("v_full")
        self.v_out = sem("v_out")
        self.sz_zero = sem("sz_zero")
        self.scan_done = sem("scan_done")
        self.sz_ready = sem("sz_ready")
        self.pads = sem("pads")
        self.pooled_ready = sem("pooled_ready")
        self.bc_ready = sem("bc_ready")
        self.w_out_ready = sem("w_out_ready")
        self.poolmm = sem("poolmm")
        self.raw_pool = sem("raw_pool")
        self.raw_conv = sem("raw_conv")
        self.sq_ready = sem("sq_ready")
        self.sq_added = sem("sq_added")
        self.ss_full = sem("ss_full")
        self.sd_ready = sem("sd_ready")
        self.yt_full = sem("yt_full")
        self.y_sq = sem("y_sq")
        self.y_in = sem("y_in")
        self.y_th = sem("y_th")
        self.z_done = sem("z_done")
        self.zt_full = sem("zt_full")
        self.zt_out = sem("zt_out")
        self.glu_full = sem("glu_full")
        self.glu_th = sem("glu_th")
        self.raw_s_ready = sem("raw_s_ready")
        self.sq_s_ready = sem("sq_s_ready")
        self.sq_s_added = sem("sq_s_added")
        self.ss_s_full = sem("ss_s_full")
        self.sd_s_ready = sem("sd_s_ready")
        self.xo_full = sem("xo_full")
        self.xo_out = sem("xo_out")
        self.x1_ready = sem("x1_ready")
        self.x1_var = sem("x1_var")
        self.x1_ss = sem("x1_ss")
        self.x1_sd = sem("x1_sd")
        self.r1_ready = sem("r1_ready")
        self.xn_ready = sem("xn_ready")
        self.xht_full = sem("xht_full")
        self.rwn_ready = sem("rwn_ready")
        self.xht_act = sem("xht_act")
        self.xht_dve = sem("xht_dve")
        self.lt_full = sem("lt_full")
        self.lt_out = sem("lt_out")
        self.lg_full = sem("lg_full")
        self.shifted = sem("shifted")
        self.exped = sem("exped")
        self.mask_ready = sem("mask_ready")
        self.pos_full = sem("pos_full")
        self.count_full = sem("count_full")
        self.flag_ready = sem("flag_ready")
        self.moved = sem("moved")
        self.now_ready = sem("now_ready")
        self.sel_ready = sem("sel_ready")
        self.hot_ready = sem("hot_ready")
        self.scat_ready = sem("scat_ready")
        self.pg_full = sem("pg_full")
        self.pg_free = sem("pg_free")
        self.t_full = sem("t_full")
        self.t_free = sem("t_free")
        self.gu_free = sem("gu_free")
        self.y_free = sem("y_free")
        self.g_ready = sem("g_ready")
        self.th_ready = sem("th_ready")
        self.h_ready = sem("h_ready")
        self.act_ready = sem("act_ready")
        self.fin_ss = sem("fin_ss")
        self.sqrt_loaded = sem("sqrt_loaded")
        self.fin_sd = sem("fin_sd")
        self.fin_y = sem("fin_y")
        self.stored = sem("stored")
        self.dve_step = sem("dve_step")
        self.act_step = sem("act_step")
        self.pool_step = sem("pool_step")
        self.eps_ready = sem("eps_ready")
        self.bias_zero = sem("bias_zero")
        self.bgh_ready = sem("bgh_ready")


def build_program(nc, x_tok, x_t, consts, cols, ssm, w_in, w_glu, w_out, b_gu, w_gu, w_dn, b_dn, fnorm, out):
    ctx = ExitStack()
    with ctx:
        def sb(name, n, dt=F32):
            return ctx.enter_context(nc.sbuf_tensor(name, [P, n], dt))

        def sem(name):
            return ctx.enter_context(nc.semaphore(name))

        ring = sb("ring", OWN_SLOTS * UNIT)
        cst = sb("cst", C_END)
        col = sb("col", V_END)
        prm = sb("prm", S_END)
        acc = sb("acc", NT * D)
        xn = sb("xn", NT * D)
        bias = sb("bias", 2 * FE)
        bdn = sb("bdn", D)
        fn = sb("fn", D)
        arena = sb("arena", 15360)
        small = sb("small", 900)
        flag = sb("flag", 1, I32)
        expi = sb("expi", NP, I32)
        ps = ctx.enter_context(nc.psum_tensor("ps", [P, 8, 512], F32))

        def at(buf, off, n):
            return buf[:, off:off + n]

        def r3(ap, a):
            return ap.rearrange("p (a b) -> p a b", a=a)

        def r4(ap, a, b):
            return ap.rearrange("p (a b c) -> p a b c", a=a, b=b)

        ident = at(cst, C_ID, 128)
        ones = at(cst, C_ONE, 128)
        below = at(cst, C_SU, 128)
        diag32 = at(cst, C_D32, 32)
        diag16 = at(cst, C_D16, 16)
        iota = at(cst, C_IOTA, SLOTS)
        rcnt = r3(at(cst, C_RC, 512), 2)

        xg = r3(at(arena, 0, 2048), NK)
        raw_pc = r3(at(arena, 0, 1024), 4)
        sq_cp = r4(at(arena, 1024, 1024), 2, 2)
        conv_y = r3(at(arena, 1024, 512), 2)
        gb = [at(arena, 2048 + 2048 * i, 2048) for i in range(2)]
        toep = at(arena, 2048, 4096).rearrange("p (j g h) -> p j g h", j=L8, g=G)
        hc = [at(arena, 6144 + 2048 * i, 2048) for i in range(2)]
        zt = at(arena, 6144, 1024)
        th2 = r3(at(arena, 7168, 1024), 4)
        raw_s = r3(at(arena, 8192, 1024), 4)
        sq_s = r3(at(arena, 9216, 1024), 4)
        gbt = at(arena, 10240, 4096).rearrange("p (g e r s) -> p g e r s", g=NP, e=2, r=2)
        vbuf = at(arena, 10240, 34 * 32)
        g1, g2, g3, zz = (at(arena, 10240 + 1024 * i, 1024) for i in range(4))
        spf = at(arena, 14336, NC * 32)
        sp = spf.rearrange("p (c r g) -> p c r g", c=NC, r=2)
        xht4 = at(arena, 0, 2048).rearrange("p (k i t) -> p i k t", k=NK, i=NT).rearrange(
            "p i (h k) t -> p i h k t", h=2)
        xht = r3(at(arena, 0, 2048), NK)
        rwn = r3(at(arena, 14336, 256), NK)
        lgt = at(arena, 12288, 256)
        rt = at(arena, 12544, 648)
        junk = at(arena, 6144, 2048)
        sqx = r3(acc[:, :], NK)
        tmp_p = at(acc, 0, 1024)
        bbar = [at(acc, 1024 + 256 * i, 256) for i in range(2)]
        c_pos = [at(prm, S_CR + 256 * i, 256) for i in range(2)]
        c_neg = [at(acc, 1536 + 256 * i, 256) for i in range(2)]
        vt_sb = at(acc, 0, 1024).rearrange("p (g r e s) -> p g r e s", g=4, r=2, e=2)
        sz = at(acc, 0, 2048).rearrange("p (r g e c) -> p r g e c", r=2, g=NP, e=2)
        xt = r3(xn[:, :], NK)
        pool_p, pool_a, pool_b = (r3(at(xn, 544 * i, 544), 2) for i in range(3))
        pooled, cgs, bgs = (r3(at(bias, 512 * i, 512), 2) for i in range(3))
        u_sb = at(bdn, 0, 1024).rearrange("p (g q c) -> p g q c", g=8, q=4)
        z_sb = at(fn, 0, 1024).rearrange("p (g j h) -> p g j h", g=8, j=L8)
        k_sb = r3(at(fn, 0, 512), 4)
        kt_sb = at(fn, 512, 512)
        conv_z = r3(at(fn, 0, 544), 2)

        n_small = [0]

        def sm(n):
            n_small[0] += n
            assert n_small[0] <= 900
            return at(small, n_small[0] - n, n)

        lr, step, mag, theta, en, ef, eq_, rang, nr, t1s, t2s, rden, u1s, u2s = (sm(16) for _ in range(14))
        trig_sc = sm(32)
        kr, ki = sm(16), sm(16)
        pow_f = sm(288)
        pw = r4(pow_f, 2, 9)
        a8 = sm(64).rearrange("p (o g i) -> p o g i", o=2, g=16)
        rcq = sm(8)
        bgh = sm(4)
        epsc = sm(2)
        r1, ss1, sd1 = sm(2), sm(4), sm(2)
        r_cp, r_s = sm(4), sm(2)
        ff_ss, ff_sd, ff_r = sm(2), sm(2), sm(2)
        dsk = r3(sm(64), 4)
        li = at(prm, S_LI, 16)
        rb_x = sb("rb_x_sb", TOK)
        rr_x = at(xn, 1632, 256)

        xtg = r3(at(arena, 0, 1024), NK)
        act_t = [at(arena, 1024 + 512 * i, 512) for i in range(2)]
        gsb, tsb, asb, hsb = ([at(arena, 6144 + 1024 * j + 512 * i, 512) for i in range(2)] for j in range(4))
        ysb = at(arena, 13328, 1024)
        sel = r4(at(arena, 14352, 256), NT, 2)
        scat = r4(at(arena, 14608, 256), NT, 2)
        scat_t = at(arena, 14864, 256)
        onehot = r3(at(arena, 15120, 128), 2)
        routes_f = at(arena, 13192, 2 * NT * (NE + 2))
        routes = r4(routes_f, 2, NT)
        posm, ghalf = (routes[:, i, :, 0:NE] for i in range(2))
        now = r4(at(arena, 15248, 8), 2, 2)

        s = Signals(sem)
        landed = [sem(f"landed{i}") for i in range(RING)]

        def vt_src(b, r):
            return ps[:, b, :].rearrange("p (g e r s) -> p g e r s", g=2, e=2, r=2)[:, :, :, r, :]

        def v_src(r):
            return ps[:, 6 + r, :].rearrange("p (g c) -> p g c", c=NC)

        def linker(eng, stepped):
            n = [0]

            def link(ins):
                n[0] += 1
                ins.then_inc(stepped, 1)
                eng.wait_ge(stepped, n[0])
            return link

        def slot(n):
            i = n % RING
            if i < OWN_SLOTS:
                return at(ring, i * UNIT, UNIT)
            return (at(prm, 0, UNIT), at(arena, 2048, UNIT), at(arena, 4096, UNIT), at(arena, 10240, UNIT))[i - OWN_SLOTS]

        def in_time(ap, pad=0):
            return ap[:, :, pad:pad + TOK].rearrange("p k (c j) -> p k j c", j=L8)

        def in_jc(ap, k):
            return ap.rearrange("p (k j c) -> p k j c", k=k, j=L8)

        w_in_k, w_out_k, w_glu_k = (w.rearrange("(k p) f -> p k f", p=P) for w in (w_in, w_out, w_glu))
        front = [(w_in_k[:, 4 * i:4 * i + 4, 0:512], 4) for i in range(2)]
        front += [(w_in_k[:, 2 * i:2 * i + 2, 512:1536], 2) for i in range(4)]
        front += [(w_out_k[:, 4 + 2 * i:6 + 2 * i, :], 2) for i in range(2)]
        front += [(w_glu_k, 4)]
        front += [(w_out_k[:, 2 * i:2 * i + 2, :], 2) for i in range(2)]
        assert len(front) == FRONT_UNITS

        block = ctx.enter_context(nc.Block())

        @block.sync
        def _(sync):
            for n, (src, k) in enumerate(front):
                if n < 2:
                    sync.dma_start(at(xn, 1024 * n, 1024), x_t[:, 1024 * n:1024 * n + 1024]).then_inc(s.ld_xt[n], 16)
                if n == 2:
                    sync.dma_start(cst[:, :], consts).then_inc(s.ld_cst, 16)
                    sync.dma_start(prm[:, S_CR:S_END], ssm[:, S_CR:S_END]).then_inc(s.ld_cs, 16)
                if n == 6:
                    sync.dma_start(col[:, V_RB:V_END], cols[:, V_RB:V_END]).then_inc(s.ld_col, 16)
                sync.dma_start(r3(slot(n), k), src).then_inc(landed[n % RING], 16)

            def stream(N, t, p):
                for u in range(PAIR_UNITS):
                    n = FRONT_UNITS + PAIR_UNITS * p + u
                    sync.wait_ge(s.unit_used, N * 2 * PAIR_UNITS + max(n - RING + 1, 1))
                    if n == OWN_SLOTS:
                        sync.wait_ge(s.hc_ready, 1)
                        sync.wait_ge(s.k_full, 1)
                    elif n == OWN_SLOTS + 1:
                        sync.wait_ge(s.yt_full, 1)
                    elif n == OWN_SLOTS + 3:
                        sync.wait_ge(s.z_done, 2)
                    if u < 16:
                        src = w_gu[bass.ds(t * 4 + (2 * p + u // 8), 1), (u % 8) * P:(u % 8 + 1) * P, :]
                        dst, src = slot(n), src.rearrange("e p f -> p (e f)")
                    else:
                        src = w_dn[bass.ds(t * 4 + (2 * p + (u - 16) // 4), 1), (u % 4) * 256:(u % 4 + 1) * 256, :]
                        dst, src = r3(slot(n), 2), src.rearrange("e (k p) f -> p (e k) f", p=P)
                    sync.dma_start(dst, src).then_inc(landed[n % RING], 16)

            with sync.Fori(0, PAIRS // 2) as t:
                for p in range(2):
                    stream(t, t, p)
            sync.wait_ge(s.flag_ready, 1)
            more = sync.value_load(flag[0:1, 0:1], min_val=0, max_val=1)
            with sync.If(more > 0):
                with sync.Fori(1, ROUNDS) as r:
                    with sync.Fori(0, PAIRS // 2) as t:
                        for p in range(2):
                            stream(r * (PAIRS // 2) + t, t, p)
            for i in range(NT):
                for h in range(2):
                    sync.wait_ge(s.fin_y, 2 * i + h + 1)
                    sync.dma_start(out[:, i, 512 * h:512 * h + 512],
                                   at(acc, 1024 * i + 512 * h, 512)).then_inc(s.stored, 16)
            sync.wait_ge(s.stored, 16 * 2 * NT)

        @block.gpsimd
        def _(pool):
            link = linker(pool, s.pool_step)
            tt = nc.gpsimd.tensor_tensor

            pool.wait_ge(s.sq_x, 2)
            link(tt(sqx[:, 0:4], sqx[:, 0:4], sqx[:, 4:8], ALU.add))
            link(tt(sqx[:, 0:2], sqx[:, 0:2], sqx[:, 2:4], ALU.add))
            tt(sqx[:, 0], sqx[:, 0], sqx[:, 1], ALU.add).then_inc(s.sq_sum, 1)

            pool.wait_ge(s.pow_ready, 1)
            pool.wait_ge(s.ld_cs, 16)
            pool.wait_ge(s.ss_x, 1)
            n8 = 8

            def of_pow(part, g0):
                return pw[:, part, 1:9, g0:g0 + n8].rearrange("p j g -> p g j").unsqueeze(3).to_broadcast([P, n8, L8, H])

            def of_c(c, g0):
                return r3(c, NP)[:, g0:g0 + n8, :].unsqueeze(2).to_broadcast([P, n8, L8, H])

            for g0 in (0, n8):
                t3 = tmp_p.rearrange("p (g j h) -> p g j h", g=n8, j=L8)
                for part, (a, b) in enumerate(((c_pos[0], c_neg[1]), (c_neg[0], c_neg[1]))):
                    o = hc[part].rearrange("p (g j h) -> p g j h", g=NP, j=L8)[:, g0:g0 + n8]
                    tt(o, of_c(a, g0), of_pow(part, g0), ALU.mult)
                    link(tt(t3, of_c(b, g0), of_pow(1 - part, g0), ALU.mult))
                    last = tt(o, o, t3, ALU.add)
                    if (g0, part) == (n8, 1):
                        last.then_inc(s.hc_ready, 1)
                        pool.wait_ge(s.hc_ready, 1)
                    else:
                        link(last)

            pool.wait_ge(s.gbt_full, 8)
            pool.wait_ge(s.k_full, 1)
            nc.gpsimd.memset(at(arena, 2048, 4096), 0.0).then_inc(s.toep_zero, 1)

            pool.wait_ge(s.ld_cst, 16)
            pool.wait_ge(s.rbx_ready, 1)
            rb = rb_x[:, :].rearrange("p (j c) -> p j c", j=L8).unsqueeze(1).to_broadcast([P, 2, L8, NC])
            pool.wait_ge(s.proj_out, 1)
            pool.wait_ge(s.pads, 1)
            link(tt(in_time(pool_p, PADT), in_time(pool_p, PADT), rb, ALU.mult))
            E_ = PADT + TOK
            link(tt(pool_a[:, :, 1:E_], pool_p[:, :, 1:E_], pool_p[:, :, 0:E_ - 1], ALU.add))
            link(tt(pool_b[:, :, 3:E_], pool_a[:, :, 3:E_], pool_a[:, :, 1:E_ - 2], ALU.add))
            tt(pooled[0:64, 0, :], pool_a[0:64, 0, PADT:], rcnt[0:64, 0, :], ALU.mult)
            link(tt(pooled[64:P, 0, :], pool_b[64:P, 0, PADT:], rcnt[64:P, 0, :], ALU.mult))
            link(tt(pool_a[:, :, 7:E_], pool_b[:, :, 7:E_], pool_b[:, :, 3:E_ - 4], ALU.add))
            link(tt(pool_b[:, :, 15:E_], pool_a[:, :, 15:E_], pool_a[:, :, 7:E_ - 8], ALU.add))
            tt(pooled[0:64, 1, :], pool_a[0:64, 1, PADT:], rcnt[0:64, 1, :], ALU.mult)
            link(tt(pooled[64:P, 1, :], pool_b[64:P, 1, PADT:], rcnt[64:P, 1, :], ALU.mult))
            tt(pooled[:, :, :], pooled[:, :, :], pool_p[:, :, PADT:], ALU.subtract).then_inc(s.pooled_ready, 1)

            pool.wait_ge(s.v_full, 2)
            nc.gpsimd.memset(acc[:, :], 0.0).then_inc(s.sz_zero, 1)

            link(tt(rr_x, rb_x[:, :], rb_x[:, :], ALU.mult))
            pool.wait_ge(s.toep_moved, 16 * L8)
            nc.gpsimd.memset(conv_z[:, :, 0:PADT], 0.0)
            pool.wait_ge(s.proj_out, 2)
            tt(bgs[:, :, :], bgs[:, :, :], rb_x[:, :].unsqueeze(1).to_broadcast([P, 2, TOK]), ALU.mult)
            pool.wait_ge(s.proj_out, 3)
            tt(cgs[:, :, :], cgs[:, :, :], rr_x.unsqueeze(1).to_broadcast([P, 2, TOK]), ALU.mult).then_inc(s.bc_ready, 1)

            pool.wait_ge(s.bc_ready, 1)
            pool.wait_ge(s.pooled_ready, 1)
            nc.gpsimd.dma_start(xn[:, :], x_tok).then_inc(s.ld_x, 16)
            pool.wait_ge(s.raw_conv, 1)
            pool.wait_ge(s.poolmm, 1)
            link(nc.gpsimd.memset(bias[:, :], 0.0))
            nc.gpsimd.dma_start(bias[0:NE, :], b_gu).then_inc(s.ld_bias, 16)
            nc.gpsimd.dma_start(fn[:, :], fnorm).then_inc(s.ld_fn, 16)
            pool.wait_ge(s.yt_full, 1)
            link(nc.gpsimd.memset(bdn[:, :], 0.0))
            nc.gpsimd.dma_start(bdn[0:NE, :], b_dn).then_inc(s.ld_bdn, 16)
            pool.wait_ge(s.ld_bdn, 16)
            tt(bdn[:, :], bdn[:, :], bdn[:, :], ALU.add).then_inc(s.bdn_ready, 1)

        @block.scalar
        def _(act):
            link = linker(act, s.act_step)
            A = nc.scalar.activation
            act.dma_start(col[:, 0:V_RB], cols[:, 0:V_RB]).then_inc(s.ld_vec, 16)
            act.dma_start(prm[:, 0:S_CR], ssm[:, 0:S_CR]).then_inc(s.ld_ssm, 16)
            for i in range(2):
                act.wait_ge(s.ld_xt[i], 16)
                if i == 0:
                    act.wait_ge(s.ld_vec, 16)
                for k in range(4 * i, 4 * i + 4):
                    A(xg[:, k, :], xt[:, k, :], ACT.Copy, scale=at(col, V_NM + k, 1)).then_inc(s.xg_ready, 1)
                A(sqx[:, 4 * i:4 * i + 4, :], xt[:, 4 * i:4 * i + 4, :], ACT.Square).then_inc(s.sq_x, 1)
            act.wait_ge(s.angle, 1)
            A(trig_sc, trig_sc, ACT.Sin).then_inc(s.trig, 1)
            act.wait_ge(s.ss_x, 1)
            act.wait_ge(s.eps_ready, 1)
            A(rb_x[:, :], ps[:, 6, 0:TOK], ACT.Sqrt, bias=epsc[:, 0:1], scale=1.0 / D).then_inc(s.sd_x, 1)

            act.wait_ge(s.unit_used, 2)
            act.wait_ge(s.rcq_ready, 1)
            for j in range(L8):
                src = ps[:, j // 4, (j % 4) * P:(j % 4 + 1) * P].rearrange("p (g h) -> p g h", g=8)
                last = A(z_sb[:, :, L8 - 1 - j, :], src, ACT.Copy, scale=rcq[:, j:j + 1])
            last.then_inc(s.z_ready, 1)

            act.wait_ge(s.pads, 1)
            act.wait_ge(s.proj_full, 1)
            for k in range(2):
                src = ps[:, 2, k * TOK:(k + 1) * TOK].rearrange("p (j c) -> p j c", j=L8)
                last = A(in_time(pool_p, PADT)[:, k], src, ACT.Copy)
            last.then_inc(s.proj_out, 1)
            act.wait_ge(s.ut_full, 1)
            A(bdn[:, :], ps[:, 6:8, :], ACT.Copy).then_inc(s.u_ready, 1)
            for n in range(4):
                act.wait_ge(s.gbt_full, 2 * n + 1)
                A(gbt[:, 4 * n:4 * n + 4, :, 0, :], ps[:, (0, 4)[n % 2], :].rearrange("p (g e s) -> p g e s", g=4, e=2),
                  ACT.Copy).then_inc(s.gbt_act, 1)
                if n == 1:
                    act.wait_ge(s.k_full, 1)
                    A(k_sb[:, :, :], ps[:, 6, :].rearrange("p (g s) -> p g s", g=4), ACT.Copy).then_inc(s.k_out, 1)
            act.wait_ge(s.kt_full, 1)
            A(kt_sb.rearrange("p (q g s) -> p g q s", q=4, g=4),
              ps[:, 7, :].rearrange("p (g q s) -> p g q s", g=4, q=4), ACT.Copy).then_inc(s.kt_out, 1)
            act.wait_ge(s.vt_full, 1)
            act.wait_ge(s.hc_ready, 1)
            for r in range(2):
                last = A(vt_sb[:, 0:2, r], vt_src(0, r), ACT.Copy)
            last.then_inc(s.vt_out, 1)
            act.wait_ge(s.v_full, 1)
            A(vbuf[:, 64:].rearrange("p (c r g) -> p r g c", c=NC, r=2)[:, 0], v_src(0), ACT.Copy).then_inc(s.v_out, 1)
            act.wait_ge(s.toep_zero, 1)
            act.wait_ge(s.kt_out, 1)
            for j in range(L8):
                n = (j + 1) * H
                act.dma_start(toep[P - n:P, j].rearrange("p g h -> p (g h)"), kt_sb[0:n, :]).then_inc(s.toep_moved, 16)
            act.wait_ge(s.proj_full, 2)
            A(bgs[:, :, :], r3(ps[:, 3, :], 2), ACT.Copy).then_inc(s.proj_out, 1)
            act.wait_ge(landed[6], 16)

            def scale_w_out(k):
                n = 9 + k // 2 if k < 4 else 4 + k // 2
                if k % 2 == 0:
                    act.wait_ge(landed[n], 16)
                w = r3(slot(n), 2)[:, k % 2, :]
                A(w, w, ACT.Copy, scale=at(col, V_BN + k, 1)).then_inc(s.w_out_ready, 1)
            scale_w_out(4)
            scale_w_out(5)
            act.wait_ge(s.proj_full, 3)
            A(cgs[:, :, :], r3(ps[:, 4, :], 2), ACT.Copy).then_inc(s.proj_out, 1)
            scale_w_out(6)
            scale_w_out(7)
            act.wait_ge(s.poolmm, 1)
            act.wait_ge(s.unit_used, 6)
            for k in range(2):
                src = ps[:, 2, k * TOK:(k + 1) * TOK]
                A(sq_cp[:, 1, k], src, ACT.Square, scale=at(col, V_PS + k, 1))
                last = A(raw_pc[:, k, :], src, ACT.Copy, scale=at(col, V_PS + k, 1))
            last.then_inc(s.raw_pool, 1)

            act.wait_ge(s.sz_zero, 1)
            act.wait_ge(s.scan_done, 1)
            A(sz[64:P, :, :, 1, :], sp[64:P].rearrange("p c r g -> p r g c"), ACT.Copy).then_inc(s.sz_ready, 1)
            act.wait_ge(s.raw_conv, 1)
            A(sq_cp[:, 0], raw_pc[:, 2:4, :], ACT.Square).then_inc(s.sq_ready, 1)
            act.wait_ge(s.ss_full, 1)
            A(r_cp, ps[:, 6, 0:4], ACT.Sqrt, bias=epsc[:, 0:1], scale=1.0 / 256).then_inc(s.sd_ready, 1)
            for b in range(2):
                act.wait_ge(s.yt_full, b + 1)
                A(at(g1, 512 * b, 512), ps[:, b, :], ACT.Square).then_inc(s.y_sq, 1)
            for b in range(2):
                act.wait_ge(s.y_in, b + 1)
                A(at(g1, 512 * b, 512), at(g3, 512 * b, 512), ACT.Tanh, scale=GELU_K).then_inc(s.y_th, 1)
            for b in range(2):
                act.wait_ge(s.zt_full, b + 1)
                o = zt.rearrange("p (q j c) -> p j q c", q=4, j=L8)[:, 4 * b:4 * b + 4]
                A(o, ps[:, 6 + b, :].rearrange("p (j q c) -> p j q c", j=4, q=4), ACT.Copy, scale=0.5).then_inc(s.zt_out, 1)
            for k in range(4):
                scale_w_out(k)
            act.wait_ge(s.bgh_ready, 1)
            for k in range(4):
                if k < 2:
                    act.wait_ge(s.glu_full, 2)
                else:
                    act.wait_ge(s.unit_used, 9)
                A(th2[:, k, :], ps[:, k // 2, (k % 2) * TOK:(k % 2 + 1) * TOK], ACT.Tanh, bias=bgh[:, k:k + 1],
                  scale=0.5).then_inc(s.glu_th, 1)
            for b in range(2):
                act.wait_ge(s.raw_s_ready, 2 * b + 2)
                A(sq_s[:, 2 * b:2 * b + 2, :], raw_s[:, 2 * b:2 * b + 2, :], ACT.Square).then_inc(s.sq_s_ready, 1)
            act.wait_ge(s.ss_s_full, 1)
            A(r_s, ps[:, 7, 0:2], ACT.Sqrt, bias=epsc[:, 1:2], scale=1.0 / 512).then_inc(s.sd_s_ready, 1)

            for m, n in enumerate(BY_HALF):
                act.wait_ge(s.x1_ready, m + 1)
                A(at(junk, 512 * n, 512), at(acc, 512 * n, 512), ACT.Square, accum_out=ss1[:, n:n + 1]).then_inc(s.x1_ss, 1)
                if m == 1:
                    for i in range(NT):
                        act.wait_ge(s.xht_full, i + 1)
                        A(xht4[:, i, 0], r3(ps[:, (0, 6)[i], :], 4), ACT.Copy).then_inc(s.xht_act, 1)
            act.wait_ge(s.x1_var, 1)
            A(sd1, sd1, ACT.Sqrt, bias=epsc[:, 0:1], scale=1.0 / D).then_inc(s.x1_sd, 1)
            act.wait_ge(s.r1_ready, 1)
            for i in range(NT):
                A(r3(xn[:, :], NT)[:, i, :], r3(acc[:, :], NT)[:, i, :], ACT.Copy, scale=r1[:, i:i + 1]).then_inc(s.xn_ready, 1)
            act.wait_ge(s.shifted, 1)
            A(at(rt, 512, 64), at(rt, 448, 64), ACT.Exp).then_inc(s.exped, 1)

            def experts(T):
                act.wait_ge(s.t_full, 3 * T + 1)
                A(scat_t, ps[:, 6, 0:TOK], ACT.Copy).then_inc(s.t_free, 1)

                def tanh(i):
                    act.wait_ge(s.g_ready, 2 * T + i + 1)
                    A(tsb[i], gsb[i], ACT.Tanh, scale=ALPHA / 2).then_inc(s.th_ready, 1)

                def act_out(i):
                    act.wait_ge(s.t_full, 3 * T + i + 2)
                    A(act_t[i], ps[:, 6, :], ACT.Copy).then_inc(s.t_free, 1)

                def y_out(i):
                    act.wait_ge(s.unit_used, FRONT_UNITS + PAIR_UNITS * T + 16 + 4 * (i + 1))
                    A(ysb[64 * i:64 * i + 64, 0:512], ps[0:64, 7, :], ACT.Copy).then_inc(s.y_free, 1)
                tanh(0)
                act_out(0)
                tanh(1)
                y_out(0)
                act_out(1)
                y_out(1)

            with act.Fori(0, PAIRS // 2) as t:
                for p in range(2):
                    experts(t * 2 + p)
            more = act.value_load(flag[0:1, 0:1], min_val=0, max_val=1)
            with act.If(more > 0):
                with act.Fori(1, ROUNDS) as r:
                    with act.Fori(0, PAIRS // 2) as t:
                        for p in range(2):
                            experts(r * PAIRS + t * 2 + p)
            A(ff_sd, epsc, ACT.Sqrt).then_inc(s.sqrt_loaded, 1)
            act.wait_ge(s.sqrt_loaded, 1)
            for i in range(NT):
                act.wait_ge(s.pg_free, more * (6 * PAIRS * (ROUNDS - 1)) + (6 * PAIRS + 2 * i))
                A(at(arena, 6144 + 1024 * i, 1024), r3(acc[:, :], NT)[:, i, :], ACT.Square, accum_out=ff_ss[:, i:i + 1]).then_inc(s.fin_ss, 1)
                act.wait_ge(s.fin_ss, i + 1)
                A(ff_sd[:, i:i + 1], ff_ss[:, i:i + 1], ACT.Sqrt, bias=epsc[:, 0:1], scale=1.0 / D).then_inc(s.fin_sd, 1)

        @block.vector
        def _(dve):
            link = linker(dve, s.dve_step)
            v = nc.vector
            TT, TS, STT = v.tensor_tensor, v.tensor_scalar, v.scalar_tensor_tensor
            v.memset(at(bias, 0, 512), 0.0).then_inc(s.bias_zero, 1)
            v.memset(epsc[:, 0:1], EPS)
            v.memset(epsc[:, 1:2], 4 * EPS).then_inc(s.eps_ready, 1)

            def exp(o, x):
                link(TS(en, x, 1.0 / math.log(2.0), MAGIC, ALU.mult, ALU.add))
                link(TS(en, en, -MAGIC, -126.0, ALU.add, ALU.max))
                TS(expi[:, :], en, 127.0, float(2 ** 23), ALU.add, ALU.mult)
                link(STT(out=ef, in0=en, scalar=-LN2_HI, in1=x, op0=ALU.mult, op1=ALU.add))
                link(STT(out=ef, in0=en, scalar=-LN2_LO, in1=ef, op0=ALU.mult, op1=ALU.add))
                link(TS(eq_, ef, 1.0 / 5040, None, ALU.mult))
                for n in (720, 120, 24, 6, 2, 1):
                    link(STT(out=eq_, in0=eq_, scalar=1.0 / n, in1=ef, op0=ALU.add, op1=ALU.mult))
                link(STT(out=o, in0=eq_, scalar=1.0, in1=expi[:, :].bitcast(F32), op0=ALU.add, op1=ALU.mult))

            dve.wait_ge(s.ld_ssm, 16)
            TS(lr, at(prm, S_LR, 16), LAMBDA_RE_MAX, None, ALU.min)
            exp(step, at(prm, S_LS, 16))
            TT(t1s, lr, step, ALU.mult)
            link(TT(theta, li, step, ALU.mult))
            sin_arg, cos_arg = trig_sc[:, 16:32], trig_sc[:, 0:16]
            link(TS(rang, theta, 1.0 / (2 * math.pi), MAGIC, ALU.mult, ALU.add))
            link(TS(rang, rang, -MAGIC, None, ALU.add))
            for c in (TWO_PI_A, TWO_PI_B, TWO_PI_C):
                link(STT(out=theta, in0=rang, scalar=-c, in1=theta, op0=ALU.mult, op1=ALU.add))
            link(TS(sin_arg, theta, 3.1415925, -3.1415925, ALU.min, ALU.max))
            link(STT(out=cos_arg, in0=sin_arg, scalar=-1.0, in1=sin_arg, op0=ALU.mult, op1=ALU.max))
            TS(cos_arg, cos_arg, -1.0, math.pi / 2, ALU.mult, ALU.add).then_inc(s.angle, 1)
            exp(mag, t1s)
            dve.wait_ge(s.trig, 1)
            v.memset(pw[:, 0, 0, :], 1.0)
            v.memset(pw[:, 1, 0, :], 0.0)
            link(TT(pw[:, :, 1, :], r3(trig_sc, 2), mag.unsqueeze(1).to_broadcast([P, 2, 16]), ALU.mult))
            ar, ai = pw[:, 0, 1, :], pw[:, 1, 1, :]

            TS(nr, ar, -1.0, None, ALU.add)
            TT(t1s, lr, lr, ALU.mult)
            link(TT(t2s, li, li, ALU.mult))
            TT(u1s, nr, lr, ALU.mult)
            TT(u2s, ai, li, ALU.mult)
            link(TT(t1s, t1s, t2s, ALU.add))
            v.reciprocal(rden, t1s)
            TT(t2s, ai, lr, ALU.mult)
            TT(kr, u1s, u2s, ALU.add)
            link(TT(ki, nr, li, ALU.mult))
            TT(kr, kr, rden, ALU.mult)
            link(TT(ki, t2s, ki, ALU.subtract))
            link(TT(ki, ki, rden, ALU.mult))
            bre, bim = r3(at(prm, S_BR, 256), NP), r3(at(prm, S_BI, 256), NP)
            krb, kib = (k.unsqueeze(2).to_broadcast([P, NP, H]) for k in (kr, ki))
            bb = [r3(b, NP) for b in bbar]
            tb = r3(spf[:, 256:512], NP), r3(spf[:, 512:768], NP)
            dve.wait_ge(s.sq_sum, 1)
            dve.wait_ge(s.ld_cs, 16)
            TS(at(acc, 1536, 512), at(prm, S_CR, 512), -1.0, None, ALU.mult)
            TS(at(prm, S_KI, 512), at(prm, S_KI, 512), -1.0, None, ALU.mult)
            TT(bb[0], bre, krb, ALU.mult)
            TT(tb[0], bim, kib, ALU.mult)
            TT(bb[1], bim, krb, ALU.mult)
            link(TT(tb[1], bre, kib, ALU.mult))
            TT(bb[0], bb[0], tb[0], ALU.subtract)
            link(TT(bb[1], bb[1], tb[1], ALU.add))

            for m in (1, 2, 4):
                lo = [pw[:, r, 1:m + 1, :] for r in range(2)]
                hi = [pw[:, r, m:m + 1, :].to_broadcast([P, m, 16]) for r in range(2)]
                o = [pw[:, r, m + 1:2 * m + 1, :] for r in range(2)]
                tp = [r3(spf[:, 768 + 64 * r:768 + 64 * r + 16 * m], m) for r in range(2)]
                TT(o[0], lo[0], hi[0], ALU.mult)
                TT(tp[0], lo[1], hi[1], ALU.mult)
                TT(o[1], lo[0], hi[1], ALU.mult)
                link(TT(tp[1], lo[1], hi[0], ALU.mult))
                TT(o[0], o[0], tp[0], ALU.subtract)
                last = TT(o[1], o[1], tp[1], ALU.add)
                if m < 4:
                    link(last)
            last.then_inc(s.pow_ready, 1)
            dve.wait_ge(s.pow_ready, 1)
            v.tensor_copy(a8[:, 0, :, 0], pw[:, 0, 8, :])
            v.tensor_copy(a8[:, 1, :, 1], pw[:, 0, 8, :])
            v.tensor_copy(a8[:, 1, :, 0], pw[:, 1, 8, :])
            TS(a8[:, 0, :, 1], pw[:, 1, 8, :], -1.0, None, ALU.mult)
            dve.wait_ge(s.ld_vec, 16)
            TS(bgh, at(col, V_BG, 4), 0.5, None, ALU.mult).then_inc(s.bgh_ready, 1)
            dve.wait_ge(s.sd_x, 1)
            dve.wait_ge(s.ld_cst, 16)
            picked = r3(at(arena, 14336, 256), L8)
            link(TT(picked, r3(rb_x[:, :], L8), diag32.unsqueeze(1).to_broadcast([P, L8, NC]), ALU.mult))
            link(v.tensor_reduce(rcq, picked, AX_X, ALU.add))
            v.reciprocal(rcq, rcq).then_inc(s.rcq_ready, 1)
            dve.wait_ge(s.rcq_ready, 1)

            for g0 in (0, 8):
                t4 = spf.rearrange("p (g t h) -> p g t h", g=8, t=L8)

                def of_pow(r):
                    return pw[:, r, 0:8, g0:g0 + 8].rearrange("p t g -> p g t").unsqueeze(3).to_broadcast([P, 8, L8, H])

                def of_b(r):
                    return bb[r][:, g0:g0 + 8, :].unsqueeze(2).to_broadcast([P, 8, L8, H])
                for r in range(2):
                    o = gb[r].rearrange("p (g t h) -> p g t h", g=NP, t=L8)[:, g0:g0 + 8]
                    TT(o, of_b(0), of_pow(r), ALU.mult)
                    link(TT(t4, of_b(1), of_pow(1 - r), ALU.mult))
                    last = TT(o, o, t4, ALU.add if r else ALU.subtract)
                    if (g0, r) == (8, 1):
                        last.then_inc(s.gb_ready, 1)
                        dve.wait_ge(s.gb_ready, 1)
                    else:
                        link(last)

            dve.wait_ge(s.xg_ready, NK)
            dve.wait_ge(s.sq_x, 2)
            v.memset(pool_p[:, :, 0:PADT], 0.0).then_inc(s.pads, 1)
            link(TT(dsk, at(col, V_DS, 4).unsqueeze(2).to_broadcast([P, 4, H]),
                    diag16.unsqueeze(1).to_broadcast([P, 4, H]), ALU.mult))
            for n in range(4):
                dve.wait_ge(s.gbt_full, 2 * n + 2)
                v.tensor_copy(gbt[:, 4 * n:4 * n + 4, :, 1, :],
                              ps[:, (1, 5)[n % 2], :].rearrange("p (g e s) -> p g e s", g=4, e=2)).then_inc(s.gbt_dve, 1)
                if n == 2:
                    dve.wait_ge(s.k_out, 1)
                    TT(k_sb[:, :, 0:H], k_sb[:, :, 0:H], dsk, ALU.add).then_inc(s.k_skip, 1)
            v.reciprocal(rb_x[:, :], rb_x[:, :]).then_inc(s.rbx_ready, 1)
            dve.wait_ge(s.hc_ready, 1)
            dve.wait_ge(s.vt_full, 1)
            for r in range(2):
                last = v.tensor_copy(vt_sb[:, 2:4, r], vt_src(1, r))
            last.then_inc(s.vt_out, 1)

            link(v.memset(sp[:, 0], 0.0))
            dve.wait_ge(s.v_full, 2)
            v.tensor_copy(vbuf[:, 64:].rearrange("p (c r g) -> p r g c", c=NC, r=2)[:, 1], v_src(1)).then_inc(s.v_out, 1)
            dve.wait_ge(s.v_out, 2)
            for c in range(NC - 1):
                terms = vbuf[:, 32 * c:32 * c + 96].rearrange("p (i x) -> p x i", i=3)
                link(TT(terms[:, :, 0:2].rearrange("p (o g) i -> p o g i", o=2), a8,
                        sp[:, c].rearrange("p r g -> p g r").unsqueeze(1).to_broadcast([P, 2, 16, 2]), ALU.mult))
                last = v.tensor_reduce(sp[:, c + 1].rearrange("p r g -> p (r g)"), terms, AX_X, ALU.add)
                if c < NC - 2:
                    link(last)
            last.then_inc(s.scan_done, 1)
            dve.wait_ge(s.scan_done, 1)
            dve.wait_ge(s.sz_zero, 1)
            v.tensor_copy(sz[0:64, :, :, 0, :], sp[0:64].rearrange("p c r g -> p r g c")).then_inc(s.sz_ready, 1)

            dve.wait_ge(s.bc_ready, 1)
            dve.wait_ge(s.unit_used, 6)
            for k in range(2):
                last = TT(in_time(conv_z, PADT)[:, k], cgs[:, k, :].rearrange("p (j c) -> p j c", j=L8),
                          ps[:, 5, k * TOK:(k + 1) * TOK].rearrange("p (j c) -> p j c", j=L8), ALU.mult)
            link(last)

            def tap(n, k):
                return conv_z[:, k, PADT - 2 + n:PADT - 2 + n + TOK], at(col, V_CW + 2 * n + k, 1)
            for k in range(2):
                last = TS(conv_y[:, k, :], *tap(2, k), None, ALU.mult)
            link(last)
            for n in (1, 0):
                for k in range(2):
                    z, w = tap(n, k)
                    last = STT(out=conv_y[:, k, :], in0=z, scalar=w, in1=conv_y[:, k, :], op0=ALU.mult, op1=ALU.add)
                link(last)
            for k in range(2):
                last = TT(raw_pc[:, 2 + k, :].rearrange("p (j c) -> p j c", j=L8), in_time(conv_y)[:, k],
                          bgs[:, k, :].rearrange("p (j c) -> p j c", j=L8), ALU.mult)
            last.then_inc(s.raw_conv, 1)
            dve.wait_ge(s.sz_ready, 2)
            dve.wait_ge(s.ld_col, 16)
            TT(rwn, r3(at(col, V_RW, NK * NE), NK), at(col, V_NF, NK).unsqueeze(2).to_broadcast([P, NK, NE]),
               ALU.mult).then_inc(s.rwn_ready, 1)
            dve.wait_ge(s.sq_ready, 1)
            TT(sq_cp[:, :, 0], sq_cp[:, :, 0], sq_cp[:, :, 1], ALU.add).then_inc(s.sq_added, 1)

            acc3, xn3 = r3(acc[:, :], NT), r3(xn[:, :], NT)
            dve.wait_ge(s.sd_ready, 1)
            link(v.reciprocal(r_cp, r_cp))
            dve.wait_ge(s.ld_x, 16)
            dve.wait_ge(s.yt_full, 2)

            def add_product(n, rms, old):
                o = slice(512 * (n % 2), 512 * (n % 2) + 512)
                return STT(out=acc3[:, n // 2, o], in0=ps[:, 2 + n, :], scalar=rms[:, n // 2:n // 2 + 1],
                           in1=old[:, n // 2, o], op0=ALU.mult, op1=ALU.add)
            for n in range(4):
                dve.wait_ge(s.xo_full, n + 1)
                add_product(n, r_cp[:, 2:4], xn3).then_inc(s.xo_out, 1)
            for b in range(2):
                h = [at(g, 512 * b, 512) for g in (g1, g2, g3, zz)]
                dve.wait_ge(s.y_sq, b + 1)
                link(TS(h[1], h[0], GELU_C, 1.0, ALU.mult, ALU.add))
                TT(h[2], ps[:, b, :], h[1], ALU.mult).then_inc(s.y_in, 1)
            for b in range(2):
                dve.wait_ge(s.y_th, b + 1)
                for g in range(4 * b, 4 * b + 4):
                    last = STT(out=zz.rearrange("p (j g h) -> p j g h", j=L8, g=8)[:, :, g, :],
                               in0=r3(at(g1, g * P, P), L8), scalar=1.0,
                               in1=r3(ps[:, b, (g % 4) * P:(g % 4 + 1) * P], L8), op0=ALU.add, op1=ALU.mult)
                last.then_inc(s.z_done, 1)
            for n in range(4):
                dve.wait_ge(s.xo_full, n + 5)
                dve.wait_ge(s.xo_out, n + 1)
                add_product(n, r_cp[:, 0:2], acc3).then_inc(s.xo_out, 1)
            dve.wait_ge(s.zt_out, 2)
            for k in range(4):
                dve.wait_ge(s.glu_th, k + 1)
                STT(out=raw_s[:, k, :], in0=th2[:, k, :], scalar=1.0, in1=zt[:, k * TOK:(k + 1) * TOK],
                    op0=ALU.add, op1=ALU.mult).then_inc(s.raw_s_ready, 1)
            dve.wait_ge(s.sq_s_ready, 2)
            link(TT(sq_s[:, 0:2], sq_s[:, 0:2], sq_s[:, 2:4], ALU.add))
            TT(sq_s[:, 0], sq_s[:, 0], sq_s[:, 1], ALU.add).then_inc(s.sq_s_added, 1)
            dve.wait_ge(s.sd_s_ready, 1)
            link(v.reciprocal(r_s, r_s))
            dve.wait_ge(s.xo_out, 8)
            for m, n in enumerate(BY_HALF):
                if m < 3:
                    dve.wait_ge(s.xo_full, 9 + m)
                else:
                    dve.wait_ge(s.unit_used, FRONT_UNITS)
                add_product(n, r_s, acc3).then_inc(s.x1_ready, 1)
            for i in range(NT):
                dve.wait_ge(s.xht_full, i + 3)
                v.tensor_copy(xht4[:, i, 1], r3(ps[:, (1, 7)[i], :], 4)).then_inc(s.xht_dve, 1)
            dve.wait_ge(s.x1_ss, 4)
            TT(sd1, ss1[:, 0:4:2], ss1[:, 1:4:2], ALU.add).then_inc(s.x1_var, 1)
            dve.wait_ge(s.x1_sd, 1)
            v.reciprocal(r1, sd1).then_inc(s.r1_ready, 1)
            dve.wait_ge(s.r1_ready, 1)

            dve.wait_ge(s.lt_full, 1)
            v.tensor_copy(lgt, ps[:, 2, 0:TOK]).then_inc(s.lt_out, 1)
            lg, gt, eq, cum, msk, v8, sh, ex, ga, ngt, den, mx = (
                at(rt, o, n) for o, n in ((0, 64), (64, 64), (128, 64), (192, 64), (256, 64), (320, 16), (448, 64),
                                          (512, 64), (576, 64), (640, 2), (642, 2), (644, 1)))
            link(v.memset(routes_f, 0.0))
            lg3, gt3, eq3, cum3, msk3, v83, sh3, ex3, ga3 = (r3(a, NT) for a in (lg, gt, eq, cum, msk, v8, sh, ex, ga))
            dve.wait_ge(s.lg_full, NT)
            for i in range(NT):
                last = STT(out=lg3[:, i, :], in0=ps[:, 3, i * NE:(i + 1) * NE], scalar=r1[:, i:i + 1],
                           in1=at(col, V_RB, NE), op0=ALU.mult, op1=ALU.add)
                if i == 0:
                    last.then_inc(s.y_free, 2)
            link(last)
            for i in range(NT):
                last = v.max(v83[:, i, :], lg3[:, i, :])
            link(last)

            def wide(a):
                return a.to_broadcast([P, NT, NE])
            TT(sh3, lg3, wide(v83[:, :, 0:1]), ALU.subtract).then_inc(s.shifted, 1)
            TT(gt3, lg3, wide(v83[:, :, 3:4]), ALU.is_gt)
            link(TT(eq3, lg3, wide(v83[:, :, 3:4]), ALU.is_equal))
            v.tensor_reduce(ngt, gt3, AX_X, ALU.add)
            for i in range(NT):
                last = v.tensor_tensor_scan(cum3[:, i, :], ones[:, 0:NE], eq3[:, i, :], 0.0, ALU.mult, ALU.add)
            link(last)
            link(TS(ngt, ngt, -1.0, float(TOPK), ALU.mult, ALU.add))
            link(TT(cum3, cum3, wide(ngt.unsqueeze(2)), ALU.is_le))
            link(TT(eq3, eq3, cum3, ALU.mult))
            TT(msk3, gt3, eq3, ALU.add).then_inc(s.mask_ready, 1)
            dve.wait_ge(s.mask_ready, 1)
            dve.wait_ge(s.exped, 1)
            link(TT(ex, ex, msk, ALU.mult))
            link(v.tensor_reduce(den, ex3, AX_X, ALU.add))
            link(TS(den, den, 2.0, None, ALU.mult))
            link(v.reciprocal(den, den))
            TT(ghalf, ex3, wide(den.unsqueeze(2)), ALU.mult)
            dve.wait_ge(s.pos_full, 1)
            link(STT(out=posm, in0=ps[:, 4, 0:64].rearrange("p (i e) -> p i e", i=NT), scalar=1.0, in1=msk3,
                     op0=ALU.add, op1=ALU.mult))

            def select(N, t):
                v.tensor_copy(now[:, :], routes[:, :, :, bass.ds(t * 2, 2)]).then_inc(s.now_ready, 1)
                dve.wait_ge(s.now_ready, N + 1)
                place, gate = (now[:, j].unsqueeze(3).to_broadcast([P, NT, 2, SLOTS]) for j in range(2))
                number = iota.unsqueeze(1).unsqueeze(1).to_broadcast([P, NT, 2, SLOTS])
                TT(sel[:, :, :, :], number, place, ALU.is_equal).then_inc(s.sel_ready, 1)
                dve.wait_ge(s.sel_ready, N + 1)
                TT(scat[:, :, :, :], sel[:, :, :, :], gate, ALU.mult).then_inc(s.scat_ready, 1)

            def pick_bias(t):
                v.tensor_copy(onehot[:, :, :], ident[:, bass.ds(t * 2, 2)].unsqueeze(2).to_broadcast(
                    [P, 2, SLOTS])).then_inc(s.hot_ready, 1)

            def experts(T, t, r):
                pick_bias(t)
                for b in range(2):
                    dve.wait_ge(s.pg_full, 6 * T + b + 1)
                    nf = at(col, V_NF + 4 * b, 4).unsqueeze(2).to_broadcast([P, 4, P])
                    last = TT(xtg[:, 4 * b:4 * b + 4, :], r3(ps[:, b, :], 4), nf, ALU.mult)
                    last.then_inc(s.pg_free, 1)
                for i in range(2):
                    dve.wait_ge(s.unit_used, FRONT_UNITS + PAIR_UNITS * T + 8 * (i + 1))
                    TS(gsb[i], ps[:, 2 + 2 * i, :], LIMIT, None, ALU.min).then_inc(s.g_ready, 1)
                    TS(asb[i], ps[:, 3 + 2 * i, :], LIMIT, -LIMIT, ALU.min, ALU.max).then_inc(s.gu_free, 1)
                    dve.wait_ge(s.th_ready, 2 * T + i + 1)
                    STT(out=hsb[i], in0=tsb[i], scalar=1.0, in1=gsb[i], op0=ALU.add, op1=ALU.mult).then_inc(s.h_ready, 1)
                    dve.wait_ge(s.h_ready, 2 * T + i + 1)
                    STT(out=asb[i], in0=asb[i], scalar=1.0, in1=hsb[i], op0=ALU.add, op1=ALU.mult).then_inc(s.act_ready, 1)
                select(T + r + 1, t + 1)
                for i in range(2):
                    dve.wait_ge(s.unit_used, FRONT_UNITS + PAIR_UNITS * T + 16 + 4 * (i + 1))
                    v.tensor_copy(ysb[64 * i:64 * i + 64, 512:1024], ps[64:P, 7, :]).then_inc(s.y_free, 1)
                dve.wait_ge(s.pg_free, 6 * T + 4)
                for n in range(4):
                    i, h = n // 2, n % 2
                    dve.wait_ge(s.pg_full, 6 * T + n + 3)
                    o = acc3[:, i, 512 * h:512 * h + 512]
                    TT(o, ps[:, n % 2, :], o, ALU.add).then_inc(s.pg_free, 1)

            select(0, 0)
            dve.wait_ge(s.count_full, 1)
            v.tensor_reduce(mx, ps[:, 5, 0:NE], AX_X, ALU.max).then_inc(s.gu_free, 2)
            dve.wait_ge(s.gu_free, 2)
            TS(flag[:, :], mx, float(SLOTS), None, ALU.is_gt).then_inc(s.flag_ready, 1)
            dve.wait_ge(s.flag_ready, 1)
            with dve.Fori(0, PAIRS // 2) as t:
                for p in range(2):
                    experts(t * 2 + p, t * 2 + p, 0)
            more = dve.value_load(flag[0:1, 0:1], min_val=0, max_val=1)
            with dve.If(more > 0):
                with dve.Fori(1, ROUNDS) as r:
                    dve.wait_ge(s.scat_ready, r * (PAIRS + 1))
                    TS(posm, posm, float(-SLOTS), None, ALU.add).then_inc(s.moved, 1)
                    dve.wait_ge(s.moved, r)
                    select(r * (PAIRS + 1), 0)
                    with dve.Fori(0, PAIRS // 2) as t:
                        for p in range(2):
                            experts(r * PAIRS + t * 2 + p, t * 2 + p, r)
            dve.wait_ge(s.ld_fn, 16)
            dve.wait_ge(s.pg_free, more * (6 * PAIRS * (ROUNDS - 1)) + (6 * PAIRS + 2))
            for i in range(NT):
                dve.wait_ge(s.fin_sd, i + 1)
                link(v.reciprocal(ff_r[:, i:i + 1], ff_sd[:, i:i + 1]))
                for h in range(2):
                    o = slice(512 * h, 512 * h + 512)
                    STT(out=acc3[:, i, o], in0=acc3[:, i, o], scalar=ff_r[:, i:i + 1], in1=fn[:, o], op0=ALU.mult,
                        op1=ALU.mult).then_inc(s.fin_y, 1)

        @block.tensor
        def _(pe):
            mm = nc.tensor.matmul

            def wait_unit(n):
                pe.wait_ge(landed[n % RING], 16)

            def keep_busy(bank, n, cols=512):
                for _ in range(n):
                    mm(ps[:, bank, 0:cols], at(bias, 0, 128), at(bias, 0, cols), start=True, stop=True)

            pe.wait_ge(s.bias_zero, 1)
            keep_busy(7, 3)
            keep_busy(7, 1, 256)
            for k in range(NK):
                wait_unit(k // 4)
                pe.wait_ge(s.xg_ready, k + 1)
                wu = r3(slot(k // 4), 4)
                for j in range(L8):
                    for q in range(4):
                        last = mm(ps[32 * q:32 * q + 32, j // 4, (j % 4) * P:(j % 4 + 1) * P],
                                  xg[:, k, j * NC:(j + 1) * NC], wu[:, k % 4, q * P:(q + 1) * P],
                                  start=(k == 0 and j % 4 == 0), stop=(k == NK - 1), skip_group_check=True)
                if k % 4 == 3:
                    last.then_inc(s.unit_used, 1)
                if k == 3:
                    pe.wait_ge(s.ld_cst, 16)
                    pe.wait_ge(s.sq_sum, 1)
                    mm(ps[:, 6, 0:TOK], ones, sqx[:, 0, :], start=True, stop=True).then_inc(s.ss_x, 1)

            def product(n, k, raw, first, last_):
                unit = 9 + k // 2 if k < 4 else 4 + k // 2
                return mm(ps[:, 2 + n, :], raw[:, k % 4, (n // 2) * P:(n // 2 + 1) * P],
                          r3(slot(unit), 2)[:, k % 2, (n % 2) * 512:(n % 2) * 512 + 512], start=first, stop=last_)

            def branch_product(n, b):
                product(n, 4 + 2 * b, raw_pc, True, False)
                product(n, 5 + 2 * b, raw_pc, False, True).then_inc(s.xo_full, 1)

            def project(f):
                for k in range(NK):
                    wait_unit(2 + k // 2)
                    last = mm(ps[:, 2 + f // 2, (f % 2) * TOK:(f % 2 + 1) * TOK],
                              r3(slot(2 + k // 2), 2)[:, k % 2, f * P:(f + 1) * P], xg[:, k, :],
                              start=(k == 0), stop=(k == NK - 1))
                if f == 7:
                    last.then_inc(s.unit_used, 4)
                elif f % 2 == 1:
                    last.then_inc(s.proj_full, 1)

            project(0)
            project(1)
            pe.wait_ge(s.z_ready, 1)
            pe.wait_ge(s.sd_x, 1)
            for g in range(8):
                last = nc.tensor.transpose(ps[:, 6 + g // 4, (g % 4) * P:(g % 4 + 1) * P],
                                           z_sb[:, g].rearrange("p j h -> p (j h)"), ident)
            last.then_inc(s.ut_full, 1)
            project(2)
            pe.wait_ge(s.gb_ready, 1)
            pe.wait_ge(s.z_ready, 1)

            def transpose_gb(n):
                if n >= 4:
                    pe.wait_ge((s.gbt_act, s.gbt_dve)[n % 2], n // 2 - 1)
                for m in range(4):
                    g = 4 * (n // 2) + m
                    last = nc.tensor.transpose(ps[:, (0, 1, 4, 5)[n % 4], m * P:(m + 1) * P],
                                               gb[n % 2][:, g * P:(g + 1) * P], ident)
                last.then_inc(s.gbt_full, 1)
            for n in range(4):
                transpose_gb(n)
            pe.wait_ge(s.u_ready, 1)
            for g4 in range(4):
                for r in range(2):
                    for q in range(4):
                        g = 4 * q + g4
                        last = mm(ps[32 * q:32 * q + 32, 6, g4 * P:(g4 + 1) * P],
                                  at(prm, (S_KR, S_KI)[r] + 32 * g, 32), gb[r][:, g * P:(g + 1) * P],
                                  start=(r == 0), stop=(r == 1))
            last.then_inc(s.k_full, 1)
            for n in range(4, 8):
                transpose_gb(n)
            project(3)
            pe.wait_ge(s.k_skip, 1)
            for g4 in range(4):
                last = nc.tensor.transpose(ps[:, 7, g4 * P:(g4 + 1) * P], k_sb[:, g4, :], ident)
            last.then_inc(s.kt_full, 1)
            pe.wait_ge(s.gbt_act, 4)
            pe.wait_ge(s.gbt_dve, 4)
            for g in range(8):
                for q in range(4):
                    last = mm(ps[32 * q:32 * q + 32, g // 4, (g % 4) * P:(g % 4 + 1) * P], u_sb[:, g, q, :],
                              gbt[:, 4 * q + g // 2, g % 2].rearrange("p r s -> p (r s)"), start=True, stop=True)
            last.then_inc(s.vt_full, 1)
            project(4)
            pe.wait_ge(s.vt_out, 2)
            pe.wait_ge(s.kt_out, 1)
            for r in range(2):
                for g in range(4):
                    o = ps[:, 6 + r, :].rearrange("p (q g c) -> p g q c", q=4, g=4)[:, g]
                    last = nc.tensor.transpose(o, vt_sb[:, g, r].rearrange("p e s -> p (e s)"), ident)
                last.then_inc(s.v_full, 1)
            project(5)
            project(6)
            pe.wait_ge(s.pooled_ready, 1)
            pe.wait_ge(s.ld_col, 16)
            pe.wait_ge(s.proj_out, 1)
            for k in range(2):
                last = mm(ps[:, 2, k * TOK:(k + 1) * TOK], at(col, V_PW + k * P, P), in_time(pooled)[:, k],
                          start=True, stop=True)
            last.then_inc(s.poolmm, 1)
            project(7)
            pe.wait_ge(s.toep_moved, 16 * L8)
            for b in range(2):
                for g in range(4 * b, 4 * b + 4):
                    for q in range(4):
                        mm(ps[32 * q:32 * q + 32, b, (g % 4) * P:(g % 4 + 1) * P], u_sb[:, g, q, :],
                           toep[:, :, 8 * q + g, :], start=(g % 4 == 0), stop=False, skip_group_check=True)
            pe.wait_ge(s.raw_pool, 1)
            pe.wait_ge(s.w_out_ready, 2)
            pe.wait_ge(s.proj_out, 3)
            for n in range(3):
                branch_product(n, 0)
            pe.wait_ge(s.sz_ready, 2)
            for b in range(2):
                for g in range(4 * b, 4 * b + 4):
                    for r in range(2):
                        for q in range(4):
                            pair = 4 * q + g // 2
                            last = mm(ps[32 * q:32 * q + 32, b, (g % 4) * P:(g % 4 + 1) * P], sz[:, r, pair, g % 2, :],
                                      hc[r][:, pair * P:(pair + 1) * P], start=False, stop=(r == 1),
                                      skip_group_check=True)
                last.then_inc(s.yt_full, 1)
            pe.wait_ge(s.sq_added, 1)
            pe.wait_ge(s.v_out, 2)
            for n in range(4):
                last = mm(ps[:, 6, n:n + 1], sq_cp[:, n // 2, 0, (n % 2) * P:(n % 2 + 1) * P], ones[:, 0:1],
                          start=True, stop=True)
            last.then_inc(s.ss_full, 1)

            def transpose_z():
                for b in range(2):
                    pe.wait_ge(s.z_done, 2)
                    if b == 0:
                        pe.wait_ge(s.sd_ready, 1)
                    for j in range(4 * b, 4 * b + 4):
                        last = nc.tensor.transpose(ps[:, 6 + b, (j % 4) * P:(j % 4 + 1) * P], zz[:, j * P:(j + 1) * P],
                                                   ident)
                    last.then_inc(s.zt_full, 1)

            pe.wait_ge(s.raw_conv, 1)
            branch_product(3, 0)
            pe.wait_ge(s.w_out_ready, 4)
            for n in range(4):
                if n == 3:
                    transpose_z()
                pe.wait_ge(s.xo_out, n + 1)
                branch_product(n, 1)
            pe.wait_ge(s.zt_out, 2)
            wait_unit(8)
            for o in range(4):
                for k in range(4):
                    last = mm(ps[:, o // 2, (o % 2) * TOK:(o % 2 + 1) * TOK], r3(slot(8), 4)[:, k, o * P:(o + 1) * P],
                              zt[:, k * TOK:(k + 1) * TOK], start=(k == 0), stop=(k == 3))
                if o < 3:
                    last.then_inc(s.glu_full, 1)
                else:
                    last.then_inc(s.unit_used, 3)
            for k in range(4):
                pe.wait_ge(s.raw_s_ready, k + 1)
                pe.wait_ge(s.w_out_ready, 5 + k)
                if k == 3:
                    pe.wait_ge(s.sq_s_added, 1)
                    for i in range(NT):
                        last = mm(ps[:, 7, i:i + 1], sq_s[:, 0, i * P:(i + 1) * P], ones[:, 0:1], start=True, stop=True)
                    last.then_inc(s.ss_s_full, 1)
                for n in range(4) if k < 3 else BY_HALF:
                    if k == 0:
                        pe.wait_ge(s.xo_out, 5 + n)
                    last = product(n, k, raw_s, k == 0, k == 3)
                    if n == 3 and k % 2 == 1:
                        last.then_inc(s.unit_used, 1)
                    elif k == 3:
                        last.then_inc(s.xo_full, 1)
            pe.wait_ge(s.glu_th, 4)
            pe.wait_ge(s.sd_s_ready, 1)
            for n, b in enumerate(BY_HALF):
                pe.wait_ge(s.x1_ready, n + 1)
                for m in range(4):
                    last = nc.tensor.transpose(ps[:, (0, 1, 6, 7)[b], m * P:(m + 1) * P],
                                               at(acc, 512 * b + m * P, P), ident)
                last.then_inc(s.xht_full, 1)
            pe.wait_ge(s.rwn_ready, 1)
            pe.wait_ge(s.x1_ready, 4)
            pe.wait_ge(s.ld_bias, 16)
            for k in range(NK):
                if k == 4:
                    keep_busy(5, 1, 256)
                pe.wait_ge(s.xht_act if k < 4 else s.xht_dve, NT)
                q = k % 4
                last = mm(ps[32 * q:32 * q + 32, 2, 0:TOK], rwn[:, k, :], xht[:, k, :],
                          start=(k < 4), stop=(k >= 4))
            last.then_inc(s.lt_full, 1)
            keep_busy(5, 2, 256)
            pe.wait_ge(s.lt_out, 1)
            for i in range(NT):
                mm(ps[:, 3, i * NE:(i + 1) * NE], lgt[:, i * P:(i + 1) * P], diag32, start=True,
                   stop=True).then_inc(s.lg_full, 1)
            keep_busy(5, 3)
            pe.wait_ge(s.mask_ready, 1)
            m01, m0, m1 = at(rt, 256, 64), at(rt, 256, 32), at(rt, 288, 32)
            mm(ps[:, 4, 0:2 * NE], below, m01, start=True, stop=False,
               skip_group_check=True).then_inc(s.pg_free, 2)
            mm(ps[:, 4, NE:2 * NE], ones, m0, start=False, stop=True, skip_group_check=True).then_inc(s.pos_full, 1)
            mm(ps[:, 5, 0:NE], ones, m0, start=True, stop=False).then_inc(s.t_free, 1)
            mm(ps[:, 5, 0:NE], ones, m1, start=False, stop=True).then_inc(s.count_full, 1)
            keep_busy(7, 2, 256)
            pe.wait_ge(s.xn_ready, NT)
            pe.wait_ge(s.bdn_ready, 1)

            def arrived(N, n):
                pe.wait_ge(landed[n % RING], (N * (2 * PAIR_UNITS // RING) + n // RING + 1) * 16)

            def experts(T, r, N, p):
                pe.wait_ge(s.sel_ready, T + r + 1)
                for b in range(2):
                    pe.wait_ge(s.pg_free, 6 * T + b + 1)
                    for k in range(4 * b, 4 * b + 4):
                        for i in range(NT):
                            last = mm(ps[:, b, (k % 4) * P:(k % 4 + 1) * P], r3(xn[:, :], NT)[:, i, k * P:(k + 1) * P],
                                      sel[:, i].rearrange("p e c -> p (e c)"),
                                      start=(i == 0), stop=(i == NT - 1))
                    last.then_inc(s.pg_full, 1)
                for e in range(2):
                    pe.wait_ge(s.gu_free, 2 * T + e + 1)
                    for k in range(NK):
                        if e == 0 and k % 4 == 0:
                            pe.wait_ge(s.pg_free, 6 * T + 3 + k // 4)
                        n = FRONT_UNITS + PAIR_UNITS * p + NK * e + k
                        arrived(N, n)
                        for b in range(2):
                            for h in range(2):
                                last = mm(ps[64 * h:64 * h + 64, 2 + 2 * e + b, :], xtg[:, k, 64 * e:64 * e + 64],
                                          slot(n)[:, FE * b + 512 * h:FE * b + 512 * h + 512],
                                          start=(k == 0), stop=(k == NK - 1))
                        last.then_inc(s.unit_used, 1)
                        if k == 0:
                            if e == 0:
                                pe.wait_ge(s.hot_ready, T + 1)
                            for b in range(2):
                                for h in range(2):
                                    mm(ps[64 * h:64 * h + 64, 2 + 2 * e + b, :], onehot[:, e, :],
                                       bias[:, FE * b + 512 * h:FE * b + 512 * h + 512], start=False, stop=False)
                    if e == 0:
                        pe.wait_ge(s.scat_ready, T + r + 1)
                        pe.wait_ge(s.t_free, 3 * T + 1)
                        for i in range(NT):
                            last = nc.tensor.transpose(ps[:, 6, i * P:(i + 1) * P], scat[:, i].rearrange("p e c -> p (e c)"), ident)
                        last.then_inc(s.t_full, 1)
                for e in range(2):
                    pe.wait_ge(s.act_ready, 2 * T + e + 1)
                    pe.wait_ge(s.t_free, 3 * T + e + 2)
                    for k in range(4):
                        last = nc.tensor.transpose(ps[:, 6, k * P:(k + 1) * P], asb[e][:, k * P:(k + 1) * P], ident)
                    last.then_inc(s.t_full, 1)
                    pe.wait_ge(s.t_free, 3 * T + e + 3)
                    pe.wait_ge(s.y_free, 4 * T + 2 * e + 2)
                    for h in range(2):
                        mm(ps[64 * h:64 * h + 64, 7, :], onehot[:, e, :], bdn[:, 512 * h:512 * h + 512],
                           start=True, stop=False)
                    for v in range(4):
                        n = FRONT_UNITS + PAIR_UNITS * p + 16 + 4 * e + v
                        arrived(N, n)
                        for m in range(2):
                            kf = 2 * v + m
                            for h in range(2):
                                last = mm(ps[64 * h:64 * h + 64, 7, :],
                                          act_t[e][:, (kf % 4) * P + (kf // 4) * 64:(kf % 4) * P + (kf // 4) * 64 + 64],
                                          r3(slot(n), 2)[:, m, 512 * h:512 * h + 512],
                                          start=False, stop=(kf == 7))
                        last.then_inc(s.unit_used, 1)
                pe.wait_ge(s.y_free, 4 * T + 6)
                for n in range(4):
                    i, h = n // 2, n % 2
                    pe.wait_ge(s.pg_free, 6 * T + n + 3)
                    mm(ps[:, n % 2, :], scat_t[:, i * P:(i + 1) * P], ysb[:, 512 * h:512 * h + 512],
                       start=True, stop=True).then_inc(s.pg_full, 1)

            with pe.Fori(0, PAIRS // 2) as t:
                for p in range(2):
                    experts(t * 2 + p, 0, t, p)
            more = pe.value_load(flag[0:1, 0:1], min_val=0, max_val=1)
            with pe.If(more > 0):
                with pe.Fori(1, ROUNDS) as r:
                    with pe.Fori(0, PAIRS // 2) as t:
                        for p in range(2):
                            experts(r * PAIRS + t * 2 + p, r, r * (PAIRS // 2) + t, p)


def kernel(x, norm_mix, w_in, ssm_lam_re, ssm_lam_im, ssm_b_re, ssm_b_im, ssm_c_re, ssm_c_im,
           ssm_d, ssm_log_step, ssm_w_glu, ssm_b_glu, pool_w, pool_scale, conv_w, branch_norm,
           w_out, norm_ffn, router_w, router_b, w_gate_up, b_gate_up, w_down, b_down, final_norm):
    import concourse.bacc as bacc
    from concourse.bass_utils import run_bass_kernel_spmd

    f = np.float32
    xp = np.asarray(x)[0].reshape(NC, L8, D).transpose(1, 0, 2).reshape(TOK, D)
    x_tok = np.ascontiguousarray(xp.reshape(NT, P, D).transpose(1, 0, 2)).reshape(P, NT * D)
    x_t = np.ascontiguousarray(xp.T.reshape(NK, P, TOK).transpose(1, 0, 2)).reshape(P, NK * TOK)

    consts = np.zeros((P, C_END), f)
    rows = np.arange(P)
    consts[:, C_ID:C_ID + P] = np.eye(P, dtype=f)
    consts[:, C_ONE:C_ONE + P] = 1
    consts[:, C_SU:C_SU + P] = rows[:, None] < rows[None, :]
    consts[:, C_D32:C_D32 + NC] = (rows % NC)[:, None] == np.arange(NC)[None, :]
    consts[:, C_D16:C_D16 + H] = (rows % H)[:, None] == np.arange(H)[None, :]
    consts[:, C_IOTA:C_IOTA + SLOTS] = np.arange(1, SLOTS + 1)[None, :]
    for k in range(2):
        for half in range(2):
            n = np.minimum(np.arange(1, TOK + 1), WINDOWS[2 * k + half])
            consts[64 * half:64 * half + 64, C_RC + k * TOK:C_RC + (k + 1) * TOK] = f(1) / n.astype(f)

    def by_chunk(v, k):
        v = np.asarray(v).reshape((k, P) + np.asarray(v).shape[1:])
        return np.moveaxis(v, 0, 1).reshape(P, -1)

    pw = np.zeros((P, 2, P), f)
    for g in range(4):
        o = 64 * (g % 2)
        pw[o:o + 64, g // 2, o:o + 64] = np.asarray(pool_w)[0, g]
    ds = np.asarray(ssm_d)[0].reshape(4, 4, 2, H).transpose(0, 2, 3, 1).reshape(P, 4)
    cols = np.concatenate([
        by_chunk(np.asarray(norm_mix)[0], NK), by_chunk(np.asarray(branch_norm)[0], NK),
        by_chunk(np.asarray(ssm_b_glu)[0], 4), by_chunk(np.asarray(pool_scale)[0], 2),
        np.asarray(conv_w)[0].reshape(3, 2, P).transpose(2, 0, 1).reshape(P, 6),
        by_chunk(np.asarray(norm_ffn)[0], NK), ds,
        np.broadcast_to(np.asarray(router_b)[0][None, :], (P, NE)),
        pw.reshape(P, 2 * P), by_chunk(np.asarray(router_w)[0], NK)], axis=1)
    assert cols.shape[1] == V_END

    def by_state(a):
        a = np.asarray(a)
        a = a.reshape((NP, 2 * ST) + a.shape[2:])
        return np.moveaxis(a, 0, 1).reshape(P, -1)

    c_re, c_im = (np.asarray(c)[0].transpose(0, 2, 1) for c in (ssm_c_re, ssm_c_im))

    def blocks(c):
        o = np.zeros((2, ST, NP, 2, H), f)
        for e in range(2):
            o[e, :, :, e, :] = c.reshape(NP, 2, ST, H)[:, e].transpose(1, 0, 2)
        return o.reshape(P, -1)

    ssm = np.concatenate([
        by_state(np.asarray(ssm_lam_re)[0]), by_state(np.asarray(ssm_lam_im)[0]),
        by_state(np.broadcast_to(np.asarray(ssm_log_step)[0][:, None], (G, ST))),
        by_state(np.asarray(ssm_b_re)[0]), by_state(np.asarray(ssm_b_im)[0]),
        by_state(c_re), by_state(c_im), blocks(c_re), blocks(c_im)], axis=1)
    assert ssm.shape[1] == S_END

    arrays = {
        "x_tok": x_tok, "x_t": x_t, "consts": consts, "cols": cols, "ssm": ssm,
        "w_in": np.asarray(w_in)[0], "w_glu": np.asarray(ssm_w_glu)[0], "w_out": np.asarray(w_out)[0],
        "b_gu": np.asarray(b_gate_up)[0], "w_gu": np.asarray(w_gate_up)[0], "w_dn": np.asarray(w_down)[0],
        "b_dn": np.asarray(b_down)[0],
        "fnorm": np.broadcast_to(np.asarray(final_norm)[None, :], (P, D)),
    }
    arrays = {k: np.ascontiguousarray(v) for k, v in arrays.items()}
    nc = bacc.Bacc("TRN2", target_bir_lowering=False, num_devices=1)
    args = [nc.dram_tensor(k, v.shape, mybir.dt.from_np(v.dtype), kind="ExternalInput").ap() for k, v in arrays.items()]
    out = nc.dram_tensor("out", (P, NT, D), F32, kind="ExternalOutput").ap()
    build_program(nc, *args, out)
    r = run_bass_kernel_spmd(nc, [arrays], core_ids=[0])
    y = r.results[0]["out"]
    return y.transpose(1, 0, 2).reshape(L8, NC, D).transpose(1, 0, 2).reshape(1, TOK, D)
```
